# Optimizing a Trainium2 kernel written in Bass

```python
import jax, jax.numpy as jnp
from jax import lax
import numpy as np

D_MODEL = 1024
BATCH = 1
SEQ = 512
DEPTH = 1

GRID_W = 64
MLA_HEADS = 8
MLA_NOPE = 64
MLA_ROPE = 32
MLA_V = 64
MLA_QK = MLA_NOPE + MLA_ROPE
Q_LORA = 256
KV_LORA = 128
MLA_WIDTH = MLA_HEADS * MLA_V
ROPE_THETA = 10000.0
Q_BLOCK = 128
NA_HEADS = 8
NA_DH = 64
NA_WIDTH = NA_HEADS * NA_DH
NA_KR_MAX = 8
NA_KC = 16
MIX_WIDTH = MLA_WIDTH + NA_WIDTH
OFF_CQ = 0
OFF_CKV = OFF_CQ + Q_LORA
OFF_KPE = OFF_CKV + KV_LORA
OFF_NA = OFF_KPE + MLA_ROPE
IN_COLS = OFF_NA + 3 * NA_WIDTH
N_GROUPS = 4
EXPERTS_PER_GROUP = 4
N_EXPERTS = N_GROUPS * EXPERTS_PER_GROUP
TOP_K_IN_GROUP = 2
D_EXPERT = 256
EPS = 1e-6

kernel_name = 'hybrid_mla_natten_hiermoe_encoder'

def rms_norm(x, g):
    xf = x.astype(jnp.float32)
    y = xf * lax.rsqrt(jnp.mean(xf * xf, axis=-1, keepdims=True) + EPS)
    return (y * g.astype(jnp.float32)).astype(x.dtype)

def rope_2d_tables(seq):
    t = jnp.arange(seq)
    row = (t // GRID_W).astype(jnp.float32)
    col = (t % GRID_W).astype(jnp.float32)
    n_freq = MLA_ROPE // 4
    inv = ROPE_THETA ** (-jnp.arange(n_freq, dtype=jnp.float32) / n_freq)
    ang_r = row[:, None] * inv[None, :]
    ang_c = col[:, None] * inv[None, :]
    return (jnp.cos(ang_r), jnp.sin(ang_r), jnp.cos(ang_c), jnp.sin(ang_c))

def _rotate(x, cos, sin):
    x1, x2 = jnp.split(x, 2, axis=-1)
    return jnp.concatenate([x1 * cos - x2 * sin, x2 * cos + x1 * sin], axis=-1)

def apply_rope_2d(x, tabs):
    cos_r, sin_r, cos_c, sin_c = [t.astype(x.dtype) for t in tabs]
    xr, xc = jnp.split(x, 2, axis=-1)
    return jnp.concatenate([_rotate(xr, cos_r, sin_r), _rotate(xc, cos_c, sin_c)], axis=-1)

def mla_mix(c_q, c_kv, k_pe, g_q_a, w_q_b, g_kv_a, w_kv_b, g_q, g_k, tabs):
    B, S, _ = c_q.shape
    q = (rms_norm(c_q, g_q_a) @ w_q_b).reshape(B, S, MLA_HEADS, MLA_QK)
    kv = (rms_norm(c_kv, g_kv_a) @ w_kv_b).reshape(B, S, MLA_HEADS, MLA_NOPE + MLA_V)
    q_nope, q_pe = q[..., :MLA_NOPE], q[..., MLA_NOPE:]
    k_nope, v = kv[..., :MLA_NOPE], kv[..., MLA_NOPE:]
    scale = MLA_QK ** -0.5
    q_nope = rms_norm(q_nope, g_q[:MLA_NOPE]) * scale
    q_pe = apply_rope_2d(rms_norm(q_pe, g_q[MLA_NOPE:]), [t[:, None, :] for t in tabs]) * scale
    k_nope = rms_norm(k_nope, g_k[:MLA_NOPE])
    k_pe = apply_rope_2d(rms_norm(k_pe, g_k[MLA_NOPE:]), tabs)
    nb = S // Q_BLOCK
    qn_b = q_nope.reshape(B, nb, Q_BLOCK, MLA_HEADS, MLA_NOPE).transpose(1, 0, 2, 3, 4)
    qp_b = q_pe.reshape(B, nb, Q_BLOCK, MLA_HEADS, MLA_ROPE).transpose(1, 0, 2, 3, 4)

    def attend(blk):
        qn, qp = blk
        s = (jnp.einsum('bqhd,bkhd->bhqk', qn, k_nope)
             + jnp.einsum('bqhr,bkr->bhqk', qp, k_pe)).astype(jnp.float32)
        p = jax.nn.softmax(s, axis=-1).astype(v.dtype)
        return jnp.einsum('bhqk,bkhd->bqhd', p, v)

    o = lax.map(attend, (qn_b, qp_b))
    return o.transpose(1, 0, 2, 3, 4).reshape(B, S, MLA_WIDTH)

def na_mix(q, k, v, g_q, g_k, rpb):
    B, S, H, dh = q.shape
    rows = S // GRID_W
    kr = min(NA_KR_MAX, rows)
    q = rms_norm(q, g_q) * (dh ** -0.5)
    k = rms_norm(k, g_k)
    qg = q.reshape(B, rows, GRID_W, H, dh).transpose(1, 0, 2, 3, 4)
    kg = k.reshape(B, rows, GRID_W, H, dh)
    vg = v.reshape(B, rows, GRID_W, H, dh)
    cols = jnp.arange(GRID_W)
    cs = jnp.clip(cols - NA_KC // 2, 0, GRID_W - NA_KC)
    col_mask = (cols[None, :] >= cs[:, None]) & (cols[None, :] < cs[:, None] + NA_KC)
    dc = jnp.clip(cols[None, :] - cols[:, None], -(NA_KC - 1), NA_KC - 1) + NA_KC - 1
    rpb_c = rpb[:, :, dc]
    neg = jnp.finfo(jnp.float32).min

    def attend_row(args):
        r, q_row = args
        rs = jnp.clip(r - kr // 2, 0, rows - kr)
        k_band = lax.dynamic_slice_in_dim(kg, rs, kr, axis=1)
        v_band = lax.dynamic_slice_in_dim(vg, rs, kr, axis=1)
        dr = rs + jnp.arange(kr) - r + NA_KR_MAX - 1
        bias = jnp.take(rpb_c, dr, axis=1).transpose(0, 2, 1, 3)
        s = jnp.einsum('bchd,bijhd->bhcij', q_row, k_band).astype(jnp.float32)
        s = jnp.where(col_mask[:, None, :], s + bias.astype(jnp.float32)[None], neg)
        p = jax.nn.softmax(s.reshape(B, H, GRID_W, kr * GRID_W), axis=-1)
        p = p.reshape(B, H, GRID_W, kr, GRID_W).astype(v.dtype)
        return jnp.einsum('bhcij,bijhd->bchd', p, v_band)

    o = lax.map(attend_row, (jnp.arange(rows), qg))
    return o.transpose(1, 0, 2, 3, 4).reshape(B, S, H * dh)

def hier_moe(h, w_rg, b_rg, w_re, b_re, w_gate, w_up, w_down):
    B, S, _ = h.shape
    hf = h.astype(jnp.float32)
    p_g = jax.nn.softmax(hf @ w_rg.astype(jnp.float32) + b_rg.astype(jnp.float32), axis=-1)
    pg_top, g_idx = lax.top_k(p_g, 1)
    le = (hf @ w_re.astype(jnp.float32) + b_re.astype(jnp.float32)).reshape(
        B, S, N_GROUPS, EXPERTS_PER_GROUP)
    g_onehot = jax.nn.one_hot(g_idx[..., 0], N_GROUPS, dtype=jnp.float32)
    le_sel = jnp.sum(le * g_onehot[..., None], axis=2)
    p_e = jax.nn.softmax(le_sel, axis=-1)
    pe_top, e_idx = lax.top_k(p_e, TOP_K_IN_GROUP)
    wts = pg_top * pe_top / jnp.sum(pe_top, axis=-1, keepdims=True)
    eid = g_idx * EXPERTS_PER_GROUP + e_idx
    combine = jnp.sum(jax.nn.one_hot(eid, N_EXPERTS, dtype=jnp.float32) * wts[..., None], axis=-2)
    a = jnp.einsum('bsd,edf->bsef', h, w_gate)
    u = jnp.einsum('bsd,edf->bsef', h, w_up)
    hid = jax.nn.silu(a) * u * combine[..., None].astype(h.dtype)
    return jnp.einsum('bsef,efd->bsd', hid, w_down)

def setup_inputs(seed: int = 0) -> dict:
    key = jax.random.key(seed)
    ks = jax.random.split(key, 24)
    L, D = DEPTH, D_MODEL
    f32 = jnp.float32

    def nrm(k, shape, scale):
        return jax.random.normal(k, shape, f32) * scale

    def gain(k, shape):
        return 1.0 + 0.05 * jax.random.normal(k, shape, f32)

    return {
        'x': jax.random.normal(ks[0], (BATCH, SEQ, D), f32),
        'g_mix_norm': gain(ks[1], (L, D)),
        'w_in': nrm(ks[2], (L, D, IN_COLS), D ** -0.5),
        'g_q_a': gain(ks[3], (L, Q_LORA)),
        'w_q_b': nrm(ks[4], (L, Q_LORA, MLA_HEADS * MLA_QK), Q_LORA ** -0.5),
        'g_kv_a': gain(ks[5], (L, KV_LORA)),
        'w_kv_b': nrm(ks[6], (L, KV_LORA, MLA_HEADS * (MLA_NOPE + MLA_V)), KV_LORA ** -0.5),
        'g_mla_q': gain(ks[7], (L, MLA_QK)),
        'g_mla_k': gain(ks[8], (L, MLA_QK)),
        'g_na_q': gain(ks[9], (L, NA_DH)),
        'g_na_k': gain(ks[10], (L, NA_DH)),
        'na_rpb': nrm(ks[11], (L, NA_HEADS, 2 * NA_KR_MAX - 1, 2 * NA_KC - 1), 0.1),
        'g_mla_out': gain(ks[12], (L, MLA_WIDTH)),
        'g_na_out': gain(ks[13], (L, NA_WIDTH)),
        'w_out': nrm(ks[14], (L, MIX_WIDTH, D), MIX_WIDTH ** -0.5),
        'g_ffn_norm': gain(ks[15], (L, D)),
        'w_router_group': nrm(ks[16], (L, D, N_GROUPS), D ** -0.5),
        'b_router_group': nrm(ks[17], (L, N_GROUPS), 0.01),
        'w_router_expert': nrm(ks[18], (L, D, N_EXPERTS), D ** -0.5),
        'b_router_expert': nrm(ks[19], (L, N_EXPERTS), 0.01),
        'w_gate': nrm(ks[20], (L, N_EXPERTS, D, D_EXPERT), D ** -0.5),
        'w_up': nrm(ks[21], (L, N_EXPERTS, D, D_EXPERT), D ** -0.5),
        'w_down': nrm(ks[22], (L, N_EXPERTS, D_EXPERT, D), D_EXPERT ** -0.5),
    }

def reference(x, g_mix_norm, w_in, g_q_a, w_q_b, g_kv_a, w_kv_b, g_mla_q, g_mla_k,
              g_na_q, g_na_k, na_rpb, g_mla_out, g_na_out, w_out, g_ffn_norm,
              w_router_group, b_router_group, w_router_expert, b_router_expert,
              w_gate, w_up, w_down):
    B, S, _ = x.shape
    tabs = rope_2d_tables(S)
    for l in range(DEPTH):
        h = rms_norm(x, g_mix_norm[l])
        proj = h @ w_in[l]
        c_q = proj[..., OFF_CQ:OFF_CKV]
        c_kv = proj[..., OFF_CKV:OFF_KPE]
        k_pe = proj[..., OFF_KPE:OFF_NA]
        na = proj[..., OFF_NA:].reshape(B, S, 3, NA_HEADS, NA_DH)
        o_a = mla_mix(c_q, c_kv, k_pe, g_q_a[l], w_q_b[l], g_kv_a[l], w_kv_b[l],
                      g_mla_q[l], g_mla_k[l], tabs)
        o_b = na_mix(na[:, :, 0], na[:, :, 1], na[:, :, 2], g_na_q[l], g_na_k[l], na_rpb[l])
        mixed = jnp.concatenate([rms_norm(o_a, g_mla_out[l]), rms_norm(o_b, g_na_out[l])], axis=-1)
        x = x + mixed @ w_out[l]
        h2 = rms_norm(x, g_ffn_norm[l])
        x = x + hier_moe(h2, w_router_group[l], b_router_group[l], w_router_expert[l],
                         b_router_expert[l], w_gate[l], w_up[l], w_down[l])
    return x


_drawn_inputs = setup_inputs


def setup_inputs(seed=0):
    import zlib

    import numpy as np

    out = dict(_drawn_inputs(seed))
    spreads = {}
    factors = {'b_router_group': 16.044, 'b_router_expert': 8.0}
    for name, (base, spread) in spreads.items():
        noise = np.random.default_rng([zlib.crc32(name.encode()), seed]).standard_normal(out[name].shape)
        drawn = base * np.exp(spread * noise) if base else spread * noise
        out[name] = __import__('jax').numpy.asarray(drawn.astype(out[name].dtype))
    for name, factor in factors.items():
        out[name] = (out[name] * factor).astype(out[name].dtype)
    return out
```

```python
import math
import numpy as np
import concourse.bass as bass
from concourse import mybir
from contextlib import ExitStack

P = 128
SEQ, D_MODEL = 512, 1024
T = SEQ // P
KD = D_MODEL // P
GRID_W = 64
ROWS = SEQ // GRID_W
TCOLS = GRID_W // T
ROPE_BASE = 10000.0
H = 8
NOPE, ROPE, DV = 64, 32, 64
QK = NOPE + ROPE
Q_LORA, KV_LORA = 256, 128
LAT = Q_LORA + KV_LORA + ROPE
DH = 64
NAW = H * DH
IN_COLS = LAT + 3 * NAW
KR_MAX, KC = 8, 16
RPB_R, RPB_C = 2 * KR_MAX - 1, 2 * KC - 1
RPB_N = H * RPB_R * RPB_C
RPB_PAD = 8
RB_RUN = (ROWS - 1) * RPB_C + 2 * KC
HALF = P // 2
WIN = [(max(P * t - HALF, 0), min(P * t + P + HALF, SEQ)) for t in range(T)]
G, EPG = 4, 4
E = G * EPG
F = 256
EPS = 1e-6
NEG = -1.0e30

C_MIX, C_LAT, C_OUT, C_FFN = 0, 8, 11, 19
C_QG, C_KG, C_NQ, C_NK = 27, 28, 29, 30
C_FFN2 = 31
NCOL = 39
R_QPE, R_KPE, R_INVN, R_INVQ, R_BIAS = 0, 32, 64, 67, 70
NROW = R_BIAS + G + E
K_TRI, K_ONE, K_CNT, K_E, K_DIG = 0, P, 2 * P, 3 * P, 3 * P + E
NK = K_DIG + 3 * T
TOP = 2
EXTRA = (TOP * SEQ - 1) // (P + 1)
FAR = 1 << 20


def build(nc, x, cols_d, rows_d, rope_d, ident_d, rpb_d, consts_d, w_in, w_qb, w_kvb, w_out, w_r,
          w_gate, w_up, w_down, out):
    fp32 = mybir.dt.float32
    ALU = mybir.AluOpType
    ACT = mybir.ActivationFunctionType
    bf16 = mybir.dt.bfloat16
    i32, u32 = mybir.dt.int32, mybir.dt.uint32
    AX = mybir.AxisListType

    ctx = ExitStack()
    with ctx:
        def sem(name):
            return ctx.enter_context(nc.semaphore(name))

        KB = 256
        arena = ctx.enter_context(nc.sbuf_tensor("arena", [P, 204 * KB], fp32))
        small = ctx.enter_context(nc.sbuf_tensor("small", [P, 980], fp32))

        def at(kb, *shape, parts=P):
            n = math.prod(shape)
            a = arena[0:parts, int(kb * KB):int(kb * KB) + n]
            if len(shape) == 2:
                return a.rearrange("p (a b) -> p a b", a=shape[0])
            if len(shape) == 3:
                return a.rearrange("p (a b c) -> p a b c", a=shape[0], b=shape[1])
            return a

        rope_cos, rope_sin = at(146.5, T, ROPE), at(203.5, T, ROPE)
        x_sb = at(0, T, D_MODEL)
        xs = at(16, T, D_MODEL)
        latT = at(16, 3, SEQ)
        kT = at(16, H, SEQ, parts=QK)
        hT = at(32, KD, SEQ)
        qT = at(32, H, SEQ, parts=QK)
        w_lat = at(48, KD, LAT)
        w_v = at(61, KD, NAW)
        w_q = at(77, KD, NAW)
        w_k = at(93, KD, NAW)
        w_o = at(77, KD, D_MODEL)
        q_sb = at(48, T, H, QK)
        k_sb = at(61, T, H, QK)
        wqb_sb = at(110, 2, H * QK)
        wkvb_sb = at(116, H * (NOPE + DV))
        bm_n = [WIN[0][1] - WIN[0][0], WIN[1][1] - WIN[1][0], WIN[T - 1][1] - WIN[T - 1][0]]
        bm = [at(120, H, bm_n[0]), at(126, H, bm_n[1]), at(134, H, bm_n[2])]
        lat = at(140, T, LAT)
        naq = at(147, T, NAW)
        nak = at(155, T, NAW)
        nav = at(163, T, NAW)
        v_sb = at(171, T, H * DV)
        rb = at(171, H, 256)
        naqT = at(179, 4, SEQ)
        nakT = at(187, 4, SEQ)
        sq = [at(195, 768), at(198, 768)]
        sq_qk = [at(23, 768), at(26, 768)]
        Pb = [at(195, 512), at(197, 512)]
        PT = [at(199, 4, P), at(201, 4, P)]
        s_bias = [at(147, 256), at(148, 256)]
        o_na = at(155, T, NAW)
        o_lat = [at(149, NAW), at(151, NAW)]
        mixT = at(120, KD, P)
        h2s = at(124, D_MODEL)
        h2T = at(128, KD, P)
        junk = at(132, D_MODEL)
        w_r_sb = at(136, KD, G + E)
        konst = at(137, NK)
        w_gu = [at(48, 2, KD, F), at(179, 2, KD, F)]
        w_dn = [at(64, 2, D_MODEL), at(110, 2, D_MODEL)]
        xg = [at(16, D_MODEL), at(20, D_MODEL)]
        xT = [at(24, KD, P), at(28, KD, P)]
        sil = [at(32, F), at(33, F)]
        hid = [at(34, F), at(35, F)]
        hidT = [at(36, 2, P), at(37, 2, P)]
        y_sb = [at(38, D_MODEL), at(42, D_MODEL)]
        hot = [at(kb, 1024).bitcast(bf16).rearrange("p (e s) -> p e s", e=E) for kb in (163, 167, 140, 93)]
        y_back = [[at(kb + 4 * i, D_MODEL) for i in (0, 1)] for kb in (77, 155, 48, 56)]
        route = at(153, T, P)
        sels = at(109, T, 64)
        x_end, x_start, x_hit, x_tmp = (at(147 + i / 16, E) for i in range(4))
        x_col = at(147.25, 16)
        x_expert = at(147.5, 8).bitcast(i32)
        ident = at(203, P)

        pos = [0]

        def sm(*shape):
            n = math.prod(shape)
            a = small[:, pos[0]:pos[0] + n]
            pos[0] += n
            if len(shape) == 2:
                a = a.rearrange("p (a b) -> p a b", a=shape[0])
            if len(shape) == 3:
                a = a.rearrange("p (a b c) -> p a b c", a=shape[0], b=shape[1])
            return a

        cols = sm(NCOL)
        rows = sm(NROW)
        ms_x = sm(T)
        rs_x = sm(T)
        ms_lat = sm(T, 3)
        rs_lat = sm(T, 3)
        ms_na = sm(2, T, H)
        rs_na = sm(2, T, H)
        ms_qk = sm(T, 3, H)
        rs_qk = sm(T, 3, H)
        mhalf = sm(32)
        kpr = sm(T, ROPE)
        rope_tmp = at(60, H * ROPE)
        kpe_tmp = sm(ROPE)
        logits = sm(T, E)
        wts = sm(T, TOP)
        slots = sm(T, TOP).bitcast(i32)
        most = sm(1)
        most_i = sm(1).bitcast(i32)
        tok_i = sm(E).bitcast(i32)
        row_i = sm(E).bitcast(i32)
        tok_f = sm(2, E)
        counts = sm(E)
        starts = sm(2, E)
        digits = sm(3 * T // 2).bitcast(bf16)
        nmax = sm(2, H)
        ssum = sm(2, 2, H)
        rsum = sm(2, 2, H)
        ms_x1 = sm(T)
        rs_x1 = sm(T)
        ms_o = sm(2, 2)
        rs_o = sm(2, 2)

        bank = [ctx.enter_context(nc.psum_tensor(f"bank{i}", [P, 512], fp32)) for i in range(8)]
        TPB = [bank[0], bank[1]]
        MMB = bank[2:6]
        SB = [bank[2], bank[3]]
        OB = [bank[4], bank[5]]
        GU = [bank[2], bank[3]]
        YR = [[bank[4], bank[5]], [bank[6], bank[7]]]
        YB = [bank[6], bank[7]]

        s_id, s_cols, s_rows, s_rope = sem("identity_in"), sem("cols_in"), sem("rows_in"), sem("rope_in")
        s_x = [sem(f"x_in{t}") for t in range(T)]
        s_win = [sem(f"w_in_in{g}") for g in range(4)]
        s_wqb, s_wkvb, s_wo, s_rb = sem("w_qb_in"), sem("w_kvb_in"), sem("w_out_in"), sem("rpb_in")
        s_wr, s_out = sem("w_router_in"), sem("out_stored")
        s_sqx, s_xs, s_hT = sem("x_squared"), sem("x_normed"), sem("hT_ready")
        s_tp = sem("transposed")
        s_tpe = [sem("bank0_read"), sem("bank1_read")]
        s_mm, s_mme = sem("projected"), sem("projection_read")
        s_sqr, s_sqf = sem("squares_ready"), sem("squares_read")
        s_latn, s_kpr, s_kpb = sem("latent_normed"), sem("kpe_rotated"), sem("kpe_spread")
        s_nan = sem("na_normed")
        s_qn, s_kn, s_qr = sem("q_normed"), sem("k_normed"), sem("q_rotated")
        s_bm, s_gc = sem("bias_ready"), sem("gains_scaled")
        s_S, s_Sr = sem("scores_ready"), sem("scores_read")
        s_mx, s_ex = sem("max_ready"), sem("probs_ready")
        s_PTr, s_pv = sem("probsT_ready"), [sem("even_pv_done"), sem("odd_pv_done")]
        s_PT = [sem("even_probsT_ready"), sem("odd_probsT_ready")]
        s_oe, s_osq, s_on = sem("attn_out_read"), sem("attn_out_squared"), sem("attn_out_normed")
        s_mixT, s_y, s_x1 = sem("mixT_ready"), sem("y_ready"), sem("x1_ready")
        s_x1sq, s_h2s, s_h2T, s_lg, s_lgr = (sem("x1_squared"), sem("h2_ready"), sem("h2T_ready"),
                                             sem("logits_ready"), sem("logits_read"))
        s_var, s_root = sem("variance_ready"), sem("root_ready")
        s_k, s_h2st, s_digits = sem("constants_in"), sem("h2_stored"), sem("digits_ready")
        s_pick, s_exps, s_sel = sem("tops_ready"), sem("top_exps_ready"), sem("choice_ready")
        s_rank, s_counted, s_most = sem("ranks_ready"), sem("experts_counted"), sem("most_ready")
        s_pass = [sem(f"dve_chain_pass{j}") for j in range(EXTRA + 1)]
        s_cnt, s_hot, s_ix, s_tok = sem("counts_ready"), sem("onehots_ready"), sem("indices_ready"), sem("tokens_ready")
        s_row, s_extra = sem("rows_ready"), sem("extra_tile_chosen")
        s_wgu = [sem("even_w_gate_up_in"), sem("odd_w_gate_up_in")]
        s_wdn = [sem("even_w_down_in"), sem("odd_w_down_in")]
        s_xg = [sem("even_rows_gathered"), sem("odd_rows_gathered")]
        s_tt, s_te = sem("expert_transposed"), sem("expert_transposes_read")
        s_gu, s_sil, s_hid = sem("gate_up_ready"), sem("silu_ready"), sem("hidden_ready")
        s_dn, s_ya, s_yv = sem("down_ready"), sem("y_left_copied"), sem("y_right_copied")
        s_yst = [sem("even_y_stored"), sem("odd_y_stored")]
        s_back, s_fin = [sem(f"y_back{t}") for t in range(T)], sem("result_ready")
        c_act, c_dve, c_pool = sem("act_chain"), sem("dve_chain"), sem("pool_chain")

        order = [("x", t, b) for t in range(T) for b in range(2)]
        order += [("lat", t, 0) for t in range(T)]
        order += [(w, t, 0) for t in range(T) for w in ("nak", "naq")]
        order += [("nap", t, h) for t in range(T) for h in range(H)]
        order += [(w, t, b) for t in range(T) for w in ("k", "q") for b in range(2)]
        for t in range(T + 1):
            for h in range(H):
                order += [("p", t, h)] if t < T else []
                order += [("mix", t - 1, 0), ("mix", t - 1, 1)] if t > 0 and h == 3 else []
                order += [("h2", t - 1, 0), ("h2", t - 1, 1)] if t > 0 and h == 7 else []
        turn = {key: n for n, key in enumerate(order)}

        def bank_read(p):
            kind, t, h = order[p]
            if kind in ("nap", "p"):
                u = (T * H if kind == "p" else 0) + t * H + h
                return s_PT[u % 2], u // 2 + 1
            return s_tpe[p % 2], sum(k[0] not in ("nap", "p") for k in order[p % 2:p + 1:2])

        roots = [("x", t) for t in range(T)] + [("lat", 0), ("nak", 0), ("naq", 0)]
        roots += [("qk", t) for t in range(T)] + [(w, t) for t in range(T) for w in ("out", "x1")]
        root = {key: n for n, key in enumerate(roots)}

        def mme_after(i):
            t, j = divmod(i - 4 * T, 4)
            return i + 1 if i < 4 * T else 4 * T + 6 * t + (1, 2, 4, 6)[j]

        h2_dram = nc.dram_tensor("h2_rows", (SEQ, D_MODEL), fp32, kind="Internal").ap()
        y_dram = nc.dram_tensor("expert_rows", (TOP * SEQ, D_MODEL), fp32, kind="Internal").ap()

        def turn_x(g, b):
            return 3 * g - 1 + b if not (isinstance(g, int) and g % E == 0) else 3 * g + b

        def turn_h(g):
            return 3 * g + 4 if not (isinstance(g, int) and g % E == E - 1) else 3 * g + 2

        def passes(eng, run, extra):
            run(0)
            eng.wait_ge(s_most, 1)
            tiles = eng.value_load(most_i[0:1, 0:1], min_val=0, max_val=EXTRA)
            for i in range(EXTRA):
                with eng.If(tiles > i):
                    extra(i)

        def extra_turns(g):
            return (3 * g, 3 * g + 1), 3 * g + 2

        def experts(eng, step):
            step(0, 0, 0)
            step(1, 1, 0)
            with eng.Fori(1, E // 2 - 1) as pair:
                step(2 * pair, 0, pair)
                step(2 * pair + 1, 1, pair)
            step(E - 2, 0, E // 2 - 1)
            step(E - 1, 1, E // 2 - 1)

        def first(e):
            return isinstance(e, int) and e == 0

        def final(e, n=1):
            return isinstance(e, int) and e >= E - n

        def x_bank(e, par, b):
            return TPB[b] if first(e) else TPB[(par + 1 + b) % 2]

        def y_stored(eng, j, e, par, half):
            if not isinstance(e, int) or E * j + e >= 2:
                eng.wait_ge(s_yst[par], 16 * (half + E // 2 * j))

        block = ctx.enter_context(nc.Block())

        def rotate(eng, link, v, c, s, tmp, n):
            c5 = c.rearrange("p (a b c) -> p a b c", a=2, b=2)
            s5 = s.rearrange("p (a b c) -> p a b c", a=2, b=2)
            tv = tmp.rearrange("p (h a b c) -> p h a b c", h=n, a=2, b=2)
            for a in range(2):
                sh = [P, n, 8]
                for b in range(2):
                    link(eng.tensor_tensor(tv[:, :, a, b, :], v[:, :, a, 1 - b, :],
                                           s5[:, a, b, :].unsqueeze(1).to_broadcast(sh), ALU.mult))
                for b in range(2):
                    link(eng.tensor_tensor(v[:, :, a, b, :], v[:, :, a, b, :],
                                           c5[:, a, b, :].unsqueeze(1).to_broadcast(sh), ALU.mult))
                    link(eng.tensor_tensor(v[:, :, a, b, :], v[:, :, a, b, :], tv[:, :, a, b, :], ALU.add))

        @block.sync
        def _(sp):
            for t in range(T):
                sp.dma_start(x_sb[:, t, :], x[t]).then_inc(s_x[t], 16)
            win = w_in.rearrange("(k p) n -> p k n", p=P)
            sp.dma_start(w_lat, win[:, :, 0:LAT]).then_inc(s_win[0], 16)
            base = RPB_PAD + (RPB_R // 2) * RPB_C + (KC // 2 - 1)
            first = RPB_N + 2 * RPB_PAD - base - RB_RUN
            for h in range(H):
                src = bass.AP(tensor=rpb_d.tensor, offset=first - h * RPB_R * RPB_C,
                              ap=[[1, TCOLS], [RPB_C, ROWS], [1, RB_RUN]])
                sp.dma_start(rb[:, h, 0:RB_RUN], src).then_inc(s_rb, 16)
            sp.dma_start(w_k, win[:, :, LAT + NAW:LAT + 2 * NAW]).then_inc(s_win[1], 16)
            sp.dma_start(w_q, win[:, :, LAT:LAT + NAW]).then_inc(s_win[2], 16)
            sp.dma_start(w_v, win[:, :, LAT + 2 * NAW:IN_COLS]).then_inc(s_win[3], 16)
            sp.dma_start(wqb_sb, w_qb.rearrange("(k p) n -> p k n", p=P)).then_inc(s_wqb, 16)
            sp.dma_start(wkvb_sb, w_kvb).then_inc(s_wkvb, 16)
            sp.wait_ge(s_mm, 3 * T)
            sp.dma_start(w_o, w_out.rearrange("(k p) n -> p k n", p=P)).then_inc(s_wo, 16)
            sp.wait_ge(s_oe, T)
            sp.dma_start(w_r_sb, w_r).then_inc(s_wr, 16)
            sp.dma_start(konst, consts_d).then_inc(s_k, 16)

            def load_gu(e, par):
                for i, w in enumerate((w_gate, w_up)):
                    sp.dma_start(w_gu[par][:, i].rearrange("p k f -> p (k f)"),
                                 row(w, e).rearrange("o (p k) f -> (o p) (k f)", p=P)).then_inc(s_wgu[par], 16)

            def load_dn(e, par):
                sp.dma_start(w_dn[par].rearrange("p k d -> p (k d)"),
                             row(w_down, e).rearrange("o (p k) d -> (o p) (k d)", p=P)).then_inc(s_wdn[par], 16)

            def row(w, e):
                return w[e:e + 1] if isinstance(e, int) else w[bass.ds(e, 1)]

            sp.wait_ge(s_tp, turn["q", T - 1, 1] + 1)
            load_gu(0, 0)
            load_dn(0, 0)
            load_gu(1, 1)
            load_dn(1, 1)
            for t in range(T):
                sp.wait_ge(s_h2s, t + 1)
                sp.dma_start(h2_dram[t * P:(t + 1) * P, :], h2s).then_inc(s_h2st, 16)

            def pass_sp(j):
                if j > 0:
                    sp.wait_ge(s_dn, 2 * E * j)
                    for par in range(2):
                        load_gu(par, par)
                        load_dn(par, par)

                def step(e, par, half):
                    g = E * j + e
                    if not final(e, 2):
                        sp.wait_ge(s_gu, g + 1)
                        load_gu(e + 2, par)
                        sp.wait_ge(s_dn, 2 * g + 2)
                        load_dn(e + 2, par)
                experts(sp, step)

            def extra_sp(i):
                g = E + i
                sp.wait_ge(s_extra, i + 1)
                sp.wait_ge(s_dn, 2 * g)
                e = sp.value_load(x_expert[0:1, i:i + 1], min_val=0, max_val=E - 1)
                load_gu(e, g % 2)
                load_dn(e, g % 2)

            passes(sp, pass_sp, extra_sp)
            for t in range(T):
                sp.wait_ge(s_fin, t + 1)
                sp.dma_start(out[t], x_sb[:, t, :]).then_inc(s_out, 16)
            sp.wait_ge(s_out, 16 * T)

        @block.gpsimd
        def _(pool):
            n = [0]

            def link(ins):
                n[0] += 1
                ins.then_inc(c_pool, 1)
                pool.wait_ge(c_pool, n[0])

            def inverse_root(key, v, n):
                pool.wait_ge(s_var, root[key] + 1)
                nc.gpsimd.tensor_tensor(v, v, mhalf[:, 0:n], ALU.pow).then_inc(s_root, 1)

            link(nc.gpsimd.memset(mhalf, -0.5))
            for t in range(T):
                inverse_root(("x", t), rs_x[:, t:t + 1], 1)

            pool.wait_ge(s_rb, 16 * H)
            for kind, off in ((0, HALF // ROWS), (1, 0), (2, 0)):
                nj = bm_n[kind] // ROWS
                v = bm[kind].rearrange("p h (c r) -> p h c r", r=ROWS)
                for lo, hi in ((0, min(nj, RPB_C - off)), (min(nj, RPB_C - off), nj)):
                    if lo < hi:
                        src = bass.AP(tensor=rb.tensor, offset=rb.offset + RB_RUN - 1 - off - lo,
                                      ap=[list(rb.ap[0]), [256, H], [-1, hi - lo], [-RPB_C, ROWS]])
                        link(nc.gpsimd.tensor_copy(v[:, :, lo:hi, :], src))
                a, b = ((0, nj), (0, nj), (0, 8))[kind]
                link(nc.gpsimd.affine_select(out=v[:, :, a:b, :], in_=v[:, :, a:b, :], compare_op=ALU.is_ge,
                                             fill=NEG, base=8 * (a + off) + 7,
                                             pattern=[[0, H], [8, b - a], [0, ROWS]], channel_multiplier=-1))
                a, b = ((16, 24), (0, nj), (0, nj))[kind]
                link(nc.gpsimd.affine_select(out=v[:, :, a:b, :], in_=v[:, :, a:b, :], compare_op=ALU.is_ge,
                                             fill=NEG, base=120 - 8 * (a + off),
                                             pattern=[[0, H], [-8, b - a], [0, ROWS]], channel_multiplier=1))
            pool.sem_inc(s_bm, 1)

            def square(i, src, width, evacs):
                pool.wait_ge(s_mme, evacs)
                if i >= 2:
                    pool.wait_ge(s_sqf, i - 1)
                nc.gpsimd.tensor_tensor(sq[i % 2][:, 0:width], src, src, ALU.mult).then_inc(s_sqr, 1)

            def flat(v):
                return v.rearrange("p a b -> p (a b)")

            def rotate_q(t):
                pool.wait_ge(s_qn, t + 1)
                rotate(nc.gpsimd, link, q_sb[:, t, :, NOPE:QK].rearrange("p h (a b c) -> p h a b c", a=2, b=2),
                       rope_cos[:, t], rope_sin[:, t], rope_tmp, H)
                pool.sem_inc(s_qr, 1)

            for t in range(T):
                square(t, lat[:, t, :], LAT, t + 1)
            inverse_root(("lat", 0), flat(rs_lat), 3 * T)
            for t in range(T):
                square(T + t, nak[:, t, :], NAW, T + t + 1)
            inverse_root(("nak", 0), flat(rs_na[:, 0]), T * H)
            for t in range(T):
                square(2 * T + t, naq[:, t, :], NAW, 2 * T + t + 1)
            inverse_root(("naq", 0), flat(rs_na[:, 1]), T * H)
            pool.wait_ge(s_rope, 32)
            for t in range(T):
                qf = q_sb[:, t, :, :].rearrange("p h d -> p (h d)")
                pool.wait_ge(s_mme, 4 * T + 6 * t + 2)
                pool.wait_ge(s_sqf, 3 * T + 2 * t - 1)
                nc.gpsimd.tensor_tensor(sq_qk[0], qf, qf, ALU.mult).then_inc(s_sqr, 1)
                pool.wait_ge(s_mme, 4 * T + 6 * t + 6)
                pool.wait_ge(s_sqf, 3 * T + 2 * t)
                nc.gpsimd.tensor_tensor(sq_qk[1][:, 0:512].rearrange("p (h d) -> p h d", h=H),
                                        k_sb[:, t, :, 0:NOPE], k_sb[:, t, :, 0:NOPE],
                                        ALU.mult).then_inc(s_sqr, 1)
                inverse_root(("qk", t), flat(rs_qk[:, t]), 3 * H)
                if t > 0:
                    rotate_q(t - 1)
            rotate_q(T - 1)
            for t in range(T):
                inverse_root(("out", t), rs_o[:, t % 2], 2)
                inverse_root(("x1", t), rs_x1[:, t:t + 1], 1)

            pool.wait_ge(s_tp, turn["p", T - 1, H - 1] + 1)
            for b in xg:
                last = nc.gpsimd.memset(b, 0.0)
            link(last)
            pool.wait_ge(s_h2st, 16 * T)

            def pass_pool(j):
                def scatter(e):
                    if e == 0:
                        pool.wait_ge(s_row, j + 1)
                    pool.wait_ge(s_ya, E * j + e + 1)
                    pool.wait_ge(s_yv, E * j + e + 1)
                    nc.gpsimd.indirect_dma_start(
                        out=y_dram, out_offset=bass.IndirectOffsetOnAxis(ap=row_i[:, e:e + 1], axis=0),
                        in_=y_sb[e % 2], in_offset=None,
                        bounds_check=TOP * SEQ - 1, oob_is_err=False).then_inc(s_yst[e % 2], 16)

                pool.wait_ge(s_tok, j + 1)

                for e in range(E):
                    g = E * j + e
                    if g >= 2:
                        pool.wait_ge(s_tt, turn_x(g - 2, 1) + 1)
                    nc.gpsimd.indirect_dma_start(
                        out=xg[e % 2], out_offset=None, in_=h2_dram,
                        in_offset=bass.IndirectOffsetOnAxis(ap=tok_i[:, e:e + 1], axis=0),
                        bounds_check=SEQ - 1, oob_is_err=False).then_inc(s_xg[e % 2], 16)
                    if e >= 3:
                        scatter(e - 3)
                scatter(E - 3)
                scatter(E - 2)
                scatter(E - 1)
                for par in range(2):
                    pool.wait_ge(s_yst[par], 16 * (E // 2) * (j + 1))

            def extra_pool(i):
                g = E + i
                pool.wait_ge(s_tok, i + 2)
                pool.wait_ge(s_tt, 3 * g)
                nc.gpsimd.indirect_dma_start(
                    out=xg[g % 2], out_offset=None, in_=h2_dram,
                    in_offset=bass.IndirectOffsetOnAxis(ap=tok_i[:, 0:1], axis=0),
                    bounds_check=SEQ - 1, oob_is_err=False).then_inc(s_xg[g % 2], 16)
                pool.wait_ge(s_row, i + 2)
                pool.wait_ge(s_ya, g + 1)
                pool.wait_ge(s_yv, g + 1)
                nc.gpsimd.indirect_dma_start(
                    out=y_dram, out_offset=bass.IndirectOffsetOnAxis(ap=row_i[:, 0:1], axis=0),
                    in_=y_sb[g % 2], in_offset=None,
                    bounds_check=TOP * SEQ - 1, oob_is_err=False).then_inc(s_yst[g % 2], 16)
                pool.wait_ge(s_yst[g % 2], 16 * (g // 2 + 1))

            passes(pool, pass_pool, extra_pool)
            for t in range(T):
                for k in range(TOP):
                    nc.gpsimd.indirect_dma_start(
                        out=y_back[t][k], out_offset=None, in_=y_dram,
                        in_offset=bass.IndirectOffsetOnAxis(ap=slots[:, t, k:k + 1], axis=0),
                        bounds_check=TOP * SEQ - 1, oob_is_err=False).then_inc(s_back[t], 16)

        @block.scalar
        def _(act):
            act.dma_start(ident, ident_d).then_inc(s_id, 16)
            act.dma_start(cols, cols_d).then_inc(s_cols, 16)
            act.dma_start(rows, rows_d.to_broadcast([P, NROW])).then_inc(s_rows, 16)
            act.dma_start(rope_cos, rope_d[0]).then_inc(s_rope, 16)
            act.dma_start(rope_sin, rope_d[1]).then_inc(s_rope, 16)
            n = [0]

            def link(ins):
                n[0] += 1
                ins.then_inc(c_act, 1)
                act.wait_ge(c_act, n[0])

            def out_squares(t):
                act.wait_ge(s_oe, T + t + 1)
                for half, o in enumerate((o_lat[t % 2], o_na[:, t, :])):
                    last = nc.scalar.activation(junk[:, half * NAW:(half + 1) * NAW], o, ACT.Square,
                                                scale=NAW ** -0.5, accum_out=ms_o[:, t % 2, half:half + 1])
                last.then_inc(s_osq, 1)

            def x1_squares(t):
                act.wait_ge(s_x1, 2 * t + 2)
                act.wait_ge(s_osq, t + 1)
                nc.scalar.activation(junk, x_sb[:, t, :], ACT.Square, scale=D_MODEL ** -0.5,
                                     accum_out=ms_x1[:, t:t + 1]).then_inc(s_x1sq, 1)

            for t in range(T):
                act.wait_ge(s_x[t], 16)
                nc.scalar.activation(xs[:, t, :], x_sb[:, t, :], ACT.Square, scale=D_MODEL ** -0.5,
                                     accum_out=ms_x[:, t:t + 1]).then_inc(s_sqx, 1)
            i = 0
            for dst, width in ((lat, LAT), (nak, NAW), (naq, NAW), (nav, NAW)):
                for t in range(T):
                    act.wait_ge(s_mm, i + 1)
                    nc.scalar.copy(dst[:, t, :], MMB[i % 4][:, 0:width]).then_inc(s_mme, 1)
                    i += 1
            act.wait_ge(s_bm, 1)
            for t in range(T):
                act.wait_ge(s_mm, i + 1)
                qf = q_sb[:, t, :, :].rearrange("p h d -> p (h d)")
                nc.scalar.copy(qf[:, 0:512], MMB[i % 4][:, 0:512]).then_inc(s_mme, 1)
                act.wait_ge(s_mm, i + 2)
                nc.scalar.copy(qf[:, 512:768], MMB[(i + 1) % 4][:, 0:256]).then_inc(s_mme, 1)
                for b in range(2):
                    act.wait_ge(s_mm, i + 3 + b)
                    src = MMB[(i + 2 + b) % 4][:, :].rearrange("p (h c) -> p h c", h=4)
                    nc.scalar.copy(k_sb[:, t, 4 * b:4 * b + 4, 0:NOPE], src[:, :, 0:NOPE]).then_inc(s_mme, 1)
                    nc.scalar.copy(v_sb[:, t, :].rearrange("p (h c) -> p h c", h=H)[:, 4 * b:4 * b + 4, :],
                                   src[:, :, NOPE:]).then_inc(s_mme, 1)
                i += 4
            act.wait_ge(s_gc, 1)
            for t in range(T):
                for w, (dst, col) in enumerate(((nakT, C_NK), (naqT, C_NQ))):
                    p = turn[("nak", "naq")[w], t, 0]
                    act.wait_ge(s_tp, p + 1)
                    nc.scalar.activation(dst[:, :, t * P:(t + 1) * P],
                                         TPB[p % 2][:, :].rearrange("p (a b) -> p a b", a=4), ACT.Copy,
                                         scale=cols[:, col:col + 1]).then_inc(s_tpe[p % 2], 1)
            for u in range(T * H):
                t, h = divmod(u, H)
                lo, hi = WIN[t]
                at0 = lo - P * max(t - 1, 0)
                act.wait_ge(s_mx, u + 1)
                if u >= 2:
                    act.wait_ge(s_tp, turn[("nap", *divmod(u - 2, H))] + 1)
                if u in (0, 1):
                    link(nc.scalar.memzero(Pb[u][:, P:3 * P].rearrange("p (a b) -> p a b", a=2)[:, :, HALF:]))
                if u in (H, H + 1):
                    link(nc.scalar.memzero(Pb[u % 2][:, 0:HALF]))
                nc.scalar.activation(Pb[u % 2][:, at0:at0 + hi - lo], s_bias[u % 2][:, 0:hi - lo], ACT.Exp,
                                     bias=nmax[:, u % 2, h:h + 1], scale=-1.0,
                                     accum_out=ssum[:, t % 2, 1, h:h + 1]).then_inc(s_ex, 1)
            for t in range(T):
                for w, (dst, col) in enumerate(((kT, C_KG), (qT, C_QG))):
                    for b in range(2):
                        p = turn[("k", "q")[w], t, b]
                        act.wait_ge(s_tp, p + 1)
                        nc.scalar.activation(dst[:, 4 * b:4 * b + 4, t * P:(t + 1) * P],
                                             TPB[p % 2][0:QK, :].rearrange("p (a b) -> p a b", a=4), ACT.Copy,
                                             scale=cols[0:QK, col:col + 1]).then_inc(s_tpe[p % 2], 1)
            for t in range(T):
                for h in range(H):
                    u = t * H + h
                    act.wait_ge(s_mx, T * H + u + 1)
                    if u >= 2:
                        act.wait_ge(s_tp, turn[("p", *divmod(u - 2, H))] + 1)
                    nc.scalar.activation(Pb[u % 2], SB[u % 2][:, :], ACT.Exp, bias=nmax[:, u % 2, h:h + 1],
                                         accum_out=ssum[:, t % 2, 0, h:h + 1]).then_inc(s_ex, 1)
                    if h == 1 and t > 0:
                        out_squares(t - 1)
                    if h == 6 and t > 0:
                        x1_squares(t - 1)
            out_squares(T - 1)
            x1_squares(T - 1)
            for t in range(T):
                act.wait_ge(s_pick, t + 1)
                r = route[:, t, :]
                nc.scalar.activation(r[:, 68:72], r[:, 0:G], ACT.Exp, bias=r[:, 73:74],
                                     accum_out=r[:, 72:73])
                nc.scalar.activation(r[:, 74:75], r[:, 33:34], ACT.Exp, bias=r[:, 75:76]).then_inc(s_exps, 1)

            def pass_act(j):
                def left_y(e, par, half):
                    act.wait_ge(s_dn, 2 * (E * j + e) + 1)
                    y_stored(act, j, e, par, half)
                    nc.scalar.copy(y_sb[par][:, 0:512], YR[par][0][:, :]).then_inc(s_ya, 1)

                def step(e, par, half):
                    g = E * j + e
                    act.wait_ge(s_gu, g + 1)
                    if not isinstance(g, int) or g >= 2:
                        act.wait_ge(s_hid, g - 1)
                    nc.scalar.activation(sil[par], GU[par][:, 0:F], ACT.Silu).then_inc(s_sil, 1)
                    if not first(e):
                        left_y(e - 1, 1 - par, half - 1 + par)
                experts(act, step)
                left_y(E - 1, 1, E // 2 - 1)

            def extra_act(i):
                g = E + i
                act.wait_ge(s_gu, g + 1)
                act.wait_ge(s_hid, g)
                nc.scalar.activation(sil[g % 2], GU[g % 2][:, 0:F], ACT.Silu).then_inc(s_sil, 1)
                act.wait_ge(s_dn, 2 * g + 1)
                act.wait_ge(s_yst[g % 2], 16 * (g // 2))
                nc.scalar.copy(y_sb[g % 2][:, 0:512], YR[g % 2][0][:, :]).then_inc(s_ya, 1)

            passes(act, pass_act, extra_act)

        @block.vector
        def _(dve):
            n = [0]

            def link(ins):
                n[0] += 1
                ins.then_inc(c_dve, 1)
                dve.wait_ge(c_dve, n[0])

            dve.wait_ge(s_cols, 16)
            link(nc.vector.tensor_scalar(cols[:, C_QG:C_QG + 1], cols[:, C_QG:C_QG + 1], QK ** -0.5, None, ALU.mult))
            nc.vector.tensor_scalar(cols[:, C_NQ:C_NQ + 1], cols[:, C_NQ:C_NQ + 1], DH ** -0.5, None,
                                    ALU.mult).then_inc(s_gc, 1)

            def wait_root(key, ins):
                ins.then_inc(s_var, 1)
                dve.wait_ge(s_root, root[key] + 1)

            def x_norm(t):
                dve.wait_ge(s_sqx, t + 1)
                wait_root(("x", t), nc.vector.tensor_scalar(rs_x[:, t:t + 1], ms_x[:, t:t + 1], EPS, None, ALU.add))
                nc.vector.tensor_scalar(xs[:, t, :], x_sb[:, t, :], rs_x[:, t:t + 1], None, ALU.mult).then_inc(s_xs, 1)

            def with_gain(dst, key, blocks, col):
                p = turn[key]
                dve.wait_ge(s_tp, p + 1)
                nc.vector.tensor_tensor(dst, TPB[p % 2][:, 0:blocks * P].rearrange("p (a b) -> p a b", a=blocks),
                                        cols[:, col:col + blocks].unsqueeze(2).to_broadcast([P, blocks, P]),
                                        ALU.mult).then_inc(s_tpe[p % 2], 1)

            for t in range(T + 1):
                if t < T:
                    x_norm(t)
                if t > 0:
                    for b in range(2):
                        with_gain(hT[:, 4 * b:4 * b + 4, (t - 1) * P:t * P], ("x", t - 1, b), 4, C_MIX + 4 * b)
            dve.wait_ge(s_rows, 16)
            for t in range(T):
                dve.wait_ge(s_sqr, t + 1)
                for j, (a, b) in enumerate(((0, Q_LORA), (Q_LORA, Q_LORA + KV_LORA), (Q_LORA + KV_LORA, LAT))):
                    last = nc.vector.tensor_reduce(ms_lat[:, t, j:j + 1], sq[t % 2][:, a:b], AX.X, ALU.add)
                last.then_inc(s_sqf, 1)
            dve.wait_ge(s_sqf, T)
            link(nc.vector.tensor_tensor(rs_lat, ms_lat, rows[:, R_INVN:R_INVN + 3].unsqueeze(1).to_broadcast([P, T, 3]),
                                         ALU.mult))
            wait_root(("lat", 0), nc.vector.tensor_scalar(rs_lat, rs_lat, EPS, None, ALU.add))
            for t in range(T):
                nc.vector.tensor_scalar(lat[:, t, 0:Q_LORA], lat[:, t, 0:Q_LORA], rs_lat[:, t, 0:1], None, ALU.mult)
                nc.vector.tensor_scalar(lat[:, t, Q_LORA:Q_LORA + KV_LORA], lat[:, t, Q_LORA:Q_LORA + KV_LORA],
                                        rs_lat[:, t, 1:2], None, ALU.mult).then_inc(s_latn, 1)
                link(nc.vector.scalar_tensor_tensor(kpr[:, t, :], lat[:, t, Q_LORA + KV_LORA:LAT], rs_lat[:, t, 2:3],
                                                    rows[:, R_KPE:R_KPE + ROPE], ALU.mult, ALU.mult))
            dve.wait_ge(s_rope, 32)
            for t in range(T):
                rotate(nc.vector, link, kpr[:, t:t + 1, :].rearrange("p h (a b c) -> p h a b c", a=2, b=2),
                       rope_cos[:, t], rope_sin[:, t], kpe_tmp, 1)

            def na_norm(w, buf):
                for t in range(T):
                    i = T + w * T + t
                    dve.wait_ge(s_sqr, i + 1)
                    nc.vector.tensor_reduce(ms_na[:, w, t, :], sq[i % 2][:, 0:NAW].rearrange("p (h d) -> p h d", h=H),
                                            AX.X, ALU.add).then_inc(s_sqf, 1)
                dve.wait_ge(s_sqf, 2 * T + w * T)
                wait_root((("nak", "naq")[w], 0),
                          nc.vector.tensor_scalar(rs_na[:, w], ms_na[:, w], 1.0 / DH, EPS, ALU.mult, ALU.add))
                for t in range(T):
                    v = buf[:, t, :].rearrange("p (h d) -> p h d", h=H)
                    nc.vector.tensor_tensor(v, v, rs_na[:, w, t, :].unsqueeze(2).to_broadcast([P, H, DH]),
                                            ALU.mult).then_inc(s_nan, 1)

            na_norm(0, nak)
            na_norm(1, naq)
            for t in range(T):
                with_gain(latT[:, :, t * P:(t + 1) * P], ("lat", t, 0), 3, C_LAT)
            def qk_means(t):
                iq, ik = 3 * T + 2 * t, 3 * T + 2 * t + 1
                dve.wait_ge(s_sqr, iq + 1)
                s3 = sq_qk[0][:, 0:H * QK].rearrange("p (h d) -> p h d", h=H)
                nc.vector.tensor_reduce(ms_qk[:, t, 0, :], s3[:, :, 0:NOPE], AX.X, ALU.add)
                nc.vector.tensor_reduce(ms_qk[:, t, 1, :], s3[:, :, NOPE:QK], AX.X, ALU.add).then_inc(s_sqf, 1)
                dve.wait_ge(s_sqr, ik + 1)
                nc.vector.tensor_reduce(ms_qk[:, t, 2, :], sq_qk[1][:, 0:512].rearrange("p (h d) -> p h d", h=H),
                                        AX.X, ALU.add).then_inc(s_sqf, 1)
                dve.wait_ge(s_sqf, ik + 1)
                link(nc.vector.tensor_tensor(rs_qk[:, t], ms_qk[:, t],
                                             rows[:, R_INVQ:R_INVQ + 3].unsqueeze(2).to_broadcast([P, 3, H]), ALU.mult))
                nc.vector.tensor_scalar(rs_qk[:, t], rs_qk[:, t], EPS, None, ALU.add).then_inc(s_var, 1)

            def qk_norm(t):
                dve.wait_ge(s_root, root["qk", t] + 1)
                pe_part = q_sb[:, t, :, NOPE:QK]
                link(nc.vector.tensor_tensor(pe_part, pe_part, rs_qk[:, t, 1, :].unsqueeze(2).to_broadcast([P, H, ROPE]),
                                             ALU.mult))
                link(nc.vector.tensor_tensor(q_sb[:, t, :, 0:NOPE], q_sb[:, t, :, 0:NOPE],
                                             rs_qk[:, t, 0, :].unsqueeze(2).to_broadcast([P, H, NOPE]), ALU.mult))
                nc.vector.tensor_tensor(pe_part, pe_part, rows[:, R_QPE:R_QPE + ROPE].unsqueeze(1).to_broadcast([P, H, ROPE]),
                                        ALU.mult).then_inc(s_qn, 1)
                nc.vector.tensor_copy(k_sb[:, t, :, NOPE:QK], kpr[:, t:t + 1, :].to_broadcast([P, H, ROPE]))
                nc.vector.tensor_tensor(k_sb[:, t, :, 0:NOPE], k_sb[:, t, :, 0:NOPE],
                                        rs_qk[:, t, 2, :].unsqueeze(2).to_broadcast([P, H, NOPE]), ALU.mult).then_inc(s_kn, 1)

            def probs_out(key, u, blocks):
                p = turn[key]
                dve.wait_ge(s_tp, p + 1)
                if u >= 2:
                    dve.wait_ge(s_pv[u % 2], u // 2)
                nc.vector.tensor_copy(PT[u % 2][:, 0:blocks, :],
                                      TPB[p % 2][:, 0:blocks * P].rearrange("p (a b) -> p a b", a=blocks))\
                    .then_inc(s_PT[u % 2], 1)

            def attn_out(t, half, units):
                dve.wait_ge(s_pv[1], units // 2)
                dve.wait_ge(s_ex, units)
                link(nc.vector.reciprocal(rsum[:, t % 2, half, :], ssum[:, t % 2, half, :]))
                ob = OB[t % 2][:, :].rearrange("p (h d) -> p h d", h=H)
                kept = o_na[:, t, :] if half else o_lat[t % 2]
                nc.vector.tensor_tensor(kept.rearrange("p (h d) -> p h d", h=H), ob,
                                        rsum[:, t % 2, half, :].unsqueeze(2).to_broadcast([P, H, DV]),
                                        ALU.mult).then_inc(s_oe, 1)

            def side(t, hh):
                if hh == 1:
                    dve.wait_ge(s_osq, t + 1)
                    wait_root(("out", t), nc.vector.tensor_scalar(rs_o[:, t % 2], ms_o[:, t % 2], EPS, None, ALU.add))
                    for half, o in enumerate((o_lat[t % 2], o_na[:, t, :])):
                        last = nc.vector.tensor_scalar(o, o, rs_o[:, t % 2, half:half + 1], None, ALU.mult)
                    last.then_inc(s_on, 1)
                if hh == 3:
                    for b in range(2):
                        with_gain(mixT[:, 4 * b:4 * b + 4, :], ("mix", t, b), 4, C_OUT + 4 * b)
                if hh == 5:
                    for b in range(2):
                        dve.wait_ge(s_y, 2 * t + b + 1)
                        xh = x_sb[:, t, b * 512:(b + 1) * 512]
                        nc.vector.tensor_tensor(xh, xh, YB[b][:, :], ALU.add).then_inc(s_x1, 1)
                if hh == 6:
                    dve.wait_ge(s_x1sq, t + 1)
                    wait_root(("x1", t), nc.vector.tensor_scalar(rs_x1[:, t:t + 1], ms_x1[:, t:t + 1], EPS, None, ALU.add))
                    if t > 0:
                        dve.wait_ge(s_h2st, 16 * t)
                    nc.vector.tensor_scalar(h2s, x_sb[:, t, :], rs_x1[:, t:t + 1], None, ALU.mult).then_inc(s_h2s, 1)
                if hh == 7:
                    for b in range(2):
                        with_gain(h2T[:, 4 * b:4 * b + 4, :], ("h2", t, b), 4, C_FFN + 4 * b)

            def logits_out(t):
                r = route[:, t, :]
                gp, ep, gm, gi, em, ei = (r[:, 8 * i:8 * i + 8] for i in range(6))
                oh, prod, gf, ef = r[:, 48:52], r[:, 52:68], r[:, 76:77], r[:, 78:80]
                link(nc.vector.memset(r[:, 0:16], NEG))
                dve.wait_ge(s_lg, t + 1)
                nc.vector.tensor_tensor(gp[:, 0:G], YB[0][:, 0:G], rows[:, R_BIAS:R_BIAS + G], ALU.add)
                nc.vector.tensor_tensor(logits[:, t, :], YB[0][:, G:G + E], rows[:, R_BIAS + G:R_BIAS + G + E],
                                        ALU.add).then_inc(s_lgr, 1)
                dve.wait_ge(s_lgr, t + 1)
                link(nc.vector.max(gm, gp))
                link(nc.vector.max_index(gi.bitcast(u32), gm, gp))
                link(nc.vector.tensor_copy(gf, gi[:, 0:1].bitcast(u32)))
                link(nc.vector.tensor_scalar(oh, konst[:, K_E:K_E + G], gf, None, ALU.is_equal))
                link(nc.vector.tensor_tensor(prod.rearrange("p (g e) -> p g e", g=G),
                                             logits[:, t, :].rearrange("p (g e) -> p g e", g=G),
                                             oh.unsqueeze(2).to_broadcast([P, G, EPG]), ALU.mult))
                link(nc.vector.tensor_reduce(ep[:, 0:EPG], prod.rearrange("p (g e) -> p e g", g=G), AX.X, ALU.add))
                link(nc.vector.max(em, ep))
                link(nc.vector.max_index(ei.bitcast(u32), em, ep))
                nc.vector.tensor_scalar(r[:, 73:74], gm[:, 0:1], -1.0, None, ALU.mult)
                nc.vector.tensor_scalar(r[:, 75:76], em[:, 0:1], -1.0, None, ALU.mult).then_inc(s_pick, 1)
                link(nc.vector.tensor_copy(ef, ei[:, 0:2].bitcast(u32)))
                link(nc.vector.tensor_scalar(gf, gf, float(EPG), None, ALU.mult))
                link(nc.vector.tensor_scalar(ef, ef, gf, None, ALU.add))
                nc.vector.tensor_scalar(r[:, 80:96], konst[:, K_E:K_E + E], ef[:, 0:1], None, ALU.is_equal)
                link(nc.vector.tensor_scalar(r[:, 96:112], konst[:, K_E:K_E + E], ef[:, 1:2], None, ALU.is_equal))
                nc.vector.tensor_tensor(sels[:, t, 0:E], r[:, 80:96], r[:, 96:112], ALU.add).then_inc(s_sel, 1)

            def ranks_out(t):
                dve.wait_ge(s_rank, t + 1)
                nc.vector.tensor_copy(sels[:, t, 2 * E:3 * E], YB[1][:, 0:E])
                nc.vector.scalar_tensor_tensor(sels[:, t, E:2 * E], YB[1][:, 0:E], 1.0, sels[:, t, 0:E],
                                               ALU.add, ALU.mult).then_inc(s_cnt, 1)
                dve.wait_ge(s_cnt, t + 1)
                onehot(t)

            def onehot(t):
                nc.vector.tensor_tensor(hot[t], konst[:, K_CNT:K_CNT + P].unsqueeze(1).to_broadcast([P, E, P]),
                                        sels[:, t, E:2 * E].unsqueeze(2).to_broadcast([P, E, P]),
                                        ALU.is_equal).then_inc(s_hot, 1)

            def weights_out(t):
                r = route[:, t, :]
                dve.wait_ge(s_exps, t + 1)
                link(nc.vector.tensor_scalar(r[:, 76:77], r[:, 74:75], 1.0, None, ALU.add))
                link(nc.vector.tensor_tensor(r[:, 77:78], r[:, 76:77], r[:, 72:73], ALU.mult))
                link(nc.vector.reciprocal(wts[:, t, 0:1], r[:, 77:78]))
                link(nc.vector.tensor_tensor(wts[:, t, 1:2], wts[:, t, 0:1], r[:, 74:75], ALU.mult))

            dve.wait_ge(s_bm, 1)
            for u in range(T * H + 1):
                if u < T * H:
                    t, h = divmod(u, H)
                    lo, hi = WIN[t]
                    kind = 0 if t == 0 else 2 if t == T - 1 else 1
                    dve.wait_ge(s_S, u + 1)
                    if u >= 2:
                        dve.wait_ge(s_ex, u - 1)
                    nc.vector.tensor_tensor_reduce(out=s_bias[u % 2][:, 0:hi - lo], in0=SB[u % 2][:, 0:hi - lo],
                                                   in1=bm[kind][:, h, :], scale=-1.0, scalar=3.0e38,
                                                   op0=ALU.add, op1=ALU.min,
                                                   accum_out=nmax[:, u % 2, h:h + 1]).then_inc(s_mx, 1)
                if u > 0:
                    tt, hh = divmod(u - 1, H)
                    if hh == 0 and tt > 0:
                        attn_out(tt - 1, 1, tt * H)
                    probs_out(("nap", tt, hh), u - 1, 2 if tt in (0, T - 1) else 3)
                    if hh == 2:
                        qk_means(tt)
                    if hh == 6:
                        qk_norm(tt)
            attn_out(T - 1, 1, T * H)

            dve.wait_ge(s_k, 16)
            nc.vector.tensor_copy(digits, konst[:, K_DIG:K_DIG + 3 * T]).then_inc(s_digits, 1)

            for u in range(T * H + 1):
                if u < T * H:
                    t, h = divmod(u, H)
                    dve.wait_ge(s_S, T * H + u + 1)
                    if u >= 2:
                        dve.wait_ge(s_ex, T * H + u - 1)
                    nc.vector.tensor_reduce(nmax[:, u % 2, h:h + 1], SB[u % 2][:, :], AX.X, ALU.max,
                                            negate=True).then_inc(s_mx, 1)
                if u > 0:
                    tt, hh = divmod(u - 1, H)
                    if hh == 0 and tt > 0:
                        attn_out(tt - 1, 0, (T + tt) * H)
                    probs_out(("p", tt, hh), T * H + u - 1, 4)
                    if tt > 0:
                        side(tt - 1, hh)
                    if tt > 1 and hh == 0:
                        logits_out(tt - 2)
                    if tt > 1 and hh == 3:
                        ranks_out(tt - 2)
            attn_out(T - 1, 0, 2 * T * H)
            logits_out(T - 2)
            for hh in range(H):
                side(T - 1, hh)
                if hh == 3:
                    ranks_out(T - 2)
            logits_out(T - 1)
            ranks_out(T - 1)
            dve.wait_ge(s_counted, 1)
            link(nc.vector.tensor_copy(counts, YB[0][:, 64:64 + E]))
            link(nc.vector.tensor_scalar(x_tmp, counts, float(P), None, ALU.is_gt))
            for j in range(2, T):
                link(nc.vector.scalar_tensor_tensor(x_tmp, counts, float(P * j), x_tmp, ALU.is_gt, ALU.add))
            a, b = x_hit, x_end
            link(nc.vector.tensor_copy(a, x_tmp))
            for shift in (1, 2, 4, 8):
                nc.vector.tensor_copy(b[:, 0:shift], a[:, 0:shift])
                link(nc.vector.tensor_tensor(b[:, shift:E], a[:, shift:E], a[:, 0:E - shift], ALU.add))
                a, b = b, a
            link(nc.vector.tensor_copy(x_end, x_hit))
            link(nc.vector.tensor_tensor(x_start, x_end, x_tmp, ALU.subtract))
            link(nc.vector.tensor_copy(most, x_end[:, E - 1:E]))
            nc.vector.tensor_copy(most_i, most).then_inc(s_most, 1)

            def slots_out():
                a, b = starts[:, 0, :], starts[:, 1, :]
                link(nc.vector.memset(a[:, 0:1], 0.0))
                link(nc.vector.tensor_copy(a[:, 1:E], counts[:, 0:E - 1]))
                for shift in (1, 2, 4, 8):
                    nc.vector.tensor_copy(b[:, 0:shift], a[:, 0:shift])
                    link(nc.vector.tensor_tensor(b[:, shift:E], a[:, shift:E], a[:, 0:E - shift], ALU.add))
                    a, b = b, a
                for t in range(T):
                    r = route[:, t, :]
                    link(nc.vector.tensor_tensor(sels[:, t, 2 * E:3 * E], sels[:, t, 2 * E:3 * E], a, ALU.add))
                    for k in range(TOP):
                        link(nc.vector.tensor_tensor_reduce(out=r[:, 112:128], in0=r[:, 80 + 16 * k:96 + 16 * k],
                                                            in1=sels[:, t, 2 * E:3 * E], scale=1.0, scalar=0.0,
                                                            op0=ALU.mult, op1=ALU.add, accum_out=r[:, 78 + k:79 + k]))
                    link(nc.vector.tensor_copy(slots[:, t, :], r[:, 78:80]))

            slots_out()

            def pass_dve(j):
                if j > 0:
                    for t in range(T):
                        v = sels[:, t, E:2 * E]
                        link_in_pass(j, nc.vector.tensor_scalar(v, v, -float(P), None, ALU.add))
                        onehot(t)
                dve.wait_ge(s_ix, j + 1)
                ix = GU[1][:, 0:3 * E].rearrange("p (e c) -> p e c", c=3)
                link_in_pass(j, nc.vector.tensor_scalar(tok_f[:, 0, :], ix[:, :, 2], -float(FAR), float(FAR),
                                                        ALU.mult, ALU.add))
                link_in_pass(j, nc.vector.scalar_tensor_tensor(tok_f[:, 1, :], ix[:, :, 1], float(P), tok_f[:, 0, :],
                                                               ALU.mult, ALU.add))
                nc.vector.tensor_tensor(tok_i, tok_f[:, 1, :], ix[:, :, 0], ALU.add).then_inc(s_tok, 1)
                dve.wait_ge(s_tok, j + 1)

                p_col = konst[:, K_DIG:K_DIG + 1]
                link_in_pass(j, nc.vector.tensor_scalar(tok_f[:, 0, :], counts, p_col, float(P * j), ALU.subtract, ALU.is_gt))
                link_in_pass(j, nc.vector.tensor_scalar(tok_f[:, 0, :], tok_f[:, 0, :], -float(FAR), float(FAR),
                                                        ALU.mult, ALU.add))
                link_in_pass(j, nc.vector.tensor_scalar(tok_f[:, 1, :], starts[:, 0, :], p_col, float(P * j),
                                                        ALU.add, ALU.add))
                for par in range(2):
                    if j > 0:
                        dve.wait_ge(s_yst[par], 16 * (E // 2) * j)
                nc.vector.tensor_tensor(row_i, tok_f[:, 0, :], tok_f[:, 1, :], ALU.add).then_inc(s_row, 1)

                def read_x(e, par):
                    g = E * j + e
                    for b in range(2):
                        dve.wait_ge(s_tt, turn_x(g, b) + 1)
                        if b == 0 and (not isinstance(g, int) or g >= 2):
                            dve.wait_ge(s_gu, g - 1)
                        nc.vector.tensor_tensor(xT[par][:, 4 * b:4 * b + 4, :],
                                                x_bank(e, par, b)[:, :].rearrange("p (a b) -> p a b", a=4),
                                                cols[:, C_FFN2 + 4 * b:C_FFN2 + 4 * b + 4].unsqueeze(2)
                                                .to_broadcast([P, 4, P]), ALU.mult).then_inc(s_te, 1)

                def right_y(e, par, half):
                    dve.wait_ge(s_dn, 2 * (E * j + e) + 2)
                    y_stored(dve, j, e, par, half)
                    nc.vector.tensor_copy(y_sb[par][:, 512:1024], YR[par][1][:, :]).then_inc(s_yv, 1)

                def step(e, par, half):
                    g = E * j + e
                    dve.wait_ge(s_sil, g + 1)
                    if not isinstance(g, int) or g >= 2:
                        dve.wait_ge(s_tt, turn_h(g - 2) + 1)
                    nc.vector.tensor_tensor(hid[par], sil[par], GU[par][:, F:2 * F], ALU.mult).then_inc(s_hid, 1)
                    if not final(e):
                        read_x(e + 1, 1 - par)
                    if not first(e):
                        right_y(e - 1, 1 - par, half - 1 + par)
                    dve.wait_ge(s_tt, turn_h(g) + 1)
                    if not isinstance(g, int) or g >= 2:
                        dve.wait_ge(s_dn, 2 * g - 2)
                    nc.vector.tensor_copy(hidT[par], TPB[par][:, 0:2 * P].rearrange("p (a b) -> p a b", a=2))\
                        .then_inc(s_te, 1)

                read_x(0, 0)
                experts(dve, step)
                right_y(E - 1, 1, E // 2 - 1)

            def link_in_pass(j, ins):
                m[j] += 1
                ins.then_inc(s_pass[j], 1)
                dve.wait_ge(s_pass[j], m[j])

            m = [0] * (EXTRA + 1)
            def extra_dve(i):
                g, par = E + i, (E + i) % 2

                def chain(ins):
                    link_in_pass(i + 1, ins)

                def picked(dst, values):
                    chain(nc.vector.tensor_tensor_reduce(out=x_tmp, in0=x_hit, in1=values, scale=1.0, scalar=0.0,
                                                         op0=ALU.mult, op1=ALU.add, accum_out=dst))

                expert, base, count, start, far, slot = (x_col[:, c:c + 1] for c in range(6))
                dve.wait_ge(s_ix, i + 1)
                chain(nc.vector.tensor_scalar(x_hit, x_start, float(i), None, ALU.is_le))
                chain(nc.vector.scalar_tensor_tensor(x_hit, x_end, float(i), x_hit, ALU.is_gt, ALU.mult))
                picked(expert, konst[:, K_E:K_E + E])
                nc.vector.tensor_copy(x_expert[:, i:i + 1], expert).then_inc(s_extra, 1)
                picked(base, x_start)
                chain(nc.vector.tensor_scalar(base, base, -float(P), float(P * (i + 1)), ALU.mult, ALU.add))
                picked(count, counts)
                picked(start, starts[:, 0, :])
                for t in range(T):
                    rank = x_col[:, 8 + t:9 + t]
                    picked(rank, sels[:, t, E:2 * E])
                    chain(nc.vector.tensor_tensor(rank, rank, base, ALU.subtract))
                    nc.vector.tensor_scalar(hot[t][:, 0, :], konst[:, K_CNT:K_CNT + P], rank, None,
                                            ALU.is_equal).then_inc(s_hot, 1)
                dve.wait_ge(s_ix, i + 2)
                ix = GU[1][:, 0:3]
                chain(nc.vector.tensor_scalar(far, ix[:, 2:3], -float(FAR), float(FAR), ALU.mult, ALU.add))
                chain(nc.vector.scalar_tensor_tensor(far, ix[:, 1:2], float(P), far, ALU.mult, ALU.add))
                nc.vector.tensor_tensor(tok_i[:, 0:1], far, ix[:, 0:1], ALU.add).then_inc(s_tok, 1)
                dve.wait_ge(s_tok, i + 2)
                p_col = konst[:, K_DIG:K_DIG + 1]
                chain(nc.vector.tensor_scalar(slot, count, p_col, base, ALU.subtract, ALU.is_gt))
                chain(nc.vector.tensor_scalar(slot, slot, -float(FAR), float(FAR), ALU.mult, ALU.add))
                chain(nc.vector.tensor_scalar(start, start, p_col, base, ALU.add, ALU.add))
                for q in range(2):
                    dve.wait_ge(s_yst[q], 16 * ((g + 1 - q) // 2))
                nc.vector.tensor_tensor(row_i[:, 0:1], slot, start, ALU.add).then_inc(s_row, 1)
                dve.wait_ge(s_row, i + 2)
                turns, turn_hid = extra_turns(g)
                for b, n in enumerate(turns):
                    dve.wait_ge(s_tt, n + 1)
                    nc.vector.tensor_tensor(xT[par][:, 4 * b:4 * b + 4, :],
                                            TPB[n % 2][:, :].rearrange("p (a b) -> p a b", a=4),
                                            cols[:, C_FFN2 + 4 * b:C_FFN2 + 4 * b + 4].unsqueeze(2)
                                            .to_broadcast([P, 4, P]), ALU.mult).then_inc(s_te, 1)
                dve.wait_ge(s_sil, g + 1)
                nc.vector.tensor_tensor(hid[par], sil[par], GU[par][:, F:2 * F], ALU.mult).then_inc(s_hid, 1)
                dve.wait_ge(s_tt, turn_hid + 1)
                nc.vector.tensor_copy(hidT[par], TPB[turn_hid % 2][:, 0:2 * P].rearrange("p (a b) -> p a b", a=2))\
                    .then_inc(s_te, 1)
                dve.wait_ge(s_dn, 2 * g + 2)
                nc.vector.tensor_copy(y_sb[par][:, 512:1024], YR[par][1][:, :]).then_inc(s_yv, 1)

            passes(dve, pass_dve, extra_dve)
            for t in range(T):
                weights_out(t)
            for t in range(T):
                dve.wait_ge(s_back[t], 32)
                for k in range(TOP):
                    ins = nc.vector.scalar_tensor_tensor(x_sb[:, t, :], y_back[t][k], wts[:, t, k:k + 1],
                                                         x_sb[:, t, :], ALU.mult, ALU.add)
                    if k == 0:
                        link(ins)
                ins.then_inc(s_fin, 1)

        @block.tensor
        def _(pe):
            def transposes(key, blocks):
                p = turn[key]
                if p >= 2:
                    pe.wait_ge(*bank_read(p - 2))
                for b, s in enumerate(blocks):
                    last = nc.tensor.transpose(TPB[p % 2][0:s.shape[-1], b * P:(b + 1) * P], s, ident)
                last.then_inc(s_tp, 1)

            def four(buf, b):
                return [buf[:, (4 * b + j) * P:(4 * b + j + 1) * P] for j in range(4)]

            pe.wait_ge(s_id, 16)
            for t in range(T):
                pe.wait_ge(s_xs, t + 1)
                for b in range(2):
                    transposes(("x", t, b), four(xs[:, t, :], b))
            i = 0
            for g, (w, width) in enumerate(((w_lat, LAT), (w_k, NAW), (w_q, NAW), (w_v, NAW))):
                pe.wait_ge(s_win[g], 16)
                for t in range(T):
                    if g == 0:
                        for b in range(2):
                            pe.wait_ge(*bank_read(turn["x", t, b]))
                    if i >= 4:
                        pe.wait_ge(s_mme, mme_after(i - 4))
                    for k in range(KD):
                        last = nc.tensor.matmul(MMB[i % 4][:, 0:width], hT[:, k, t * P:(t + 1) * P], w[:, k, :],
                                                start=(k == 0), stop=(k == KD - 1))
                    last.then_inc(s_mm, 1)
                    i += 1
            for t in range(T):
                pe.wait_ge(s_latn, t + 1)
                transposes(("lat", t, 0), [lat[:, t, k * P:(k + 1) * P] for k in range(3)])
            pe.wait_ge(s_wqb, 16)
            pe.wait_ge(s_wkvb, 16)
            for t in range(T):
                p = turn["lat", t, 0]
                pe.wait_ge(*bank_read(p))
                for lo, hi, w in ((0, 512, "q"), (512, H * QK, "q"), (0, 512, "kv"), (512, H * (NOPE + DV), "kv")):
                    pe.wait_ge(s_mme, mme_after(i - 4))
                    for k in ((0, 1) if w == "q" else (2,)):
                        rhs = wqb_sb[:, k, lo:hi] if w == "q" else wkvb_sb[:, lo:hi]
                        last = nc.tensor.matmul(MMB[i % 4][:, 0:hi - lo], latT[:, k, t * P:(t + 1) * P], rhs,
                                                start=(k != 1), stop=(k != 0))
                    last.then_inc(s_mm, 1)
                    i += 1
            for t in range(T):
                for w, (name, buf) in enumerate((("nak", nak), ("naq", naq))):
                    pe.wait_ge(s_nan, w * T + t + 1)
                    transposes((name, t, 0), four(buf[:, t, :], 0))

            def na_scores(u):
                t, h = divmod(u, H)
                lo, hi = WIN[t]
                r = HALF * (h % 2)
                if u >= 2:
                    pe.wait_ge(s_mx, u - 1)
                nc.tensor.matmul(SB[u % 2][:, 0:hi - lo], naqT[r:r + DH, h // 2, t * P:(t + 1) * P],
                                 nakT[r:r + DH, h // 2, lo:hi], start=True, stop=True).then_inc(s_S, 1)

            def na_values(u):
                t, h = divmod(u, H)
                if h == 0 and t >= 2:
                    pe.wait_ge(s_oe, t - 1)
                pe.wait_ge(s_PT[u % 2], u // 2 + 1)
                kt0 = max(t - 1, 0)
                nb = 2 if t in (0, T - 1) else 3
                for b in range(nb):
                    last = nc.tensor.matmul(OB[t % 2][:, h * DV:(h + 1) * DV], PT[u % 2][:, b, :],
                                            nav[:, kt0 + b, h * DH:(h + 1) * DH],
                                            start=(b == 0), stop=(b == nb - 1))
                last.then_inc(s_pv[u % 2], 1)

            pe.wait_ge(s_mme, mme_after(8 * T - 1))
            for t in range(T):
                for name in ("nak", "naq"):
                    p = turn[name, t, 0]
                    pe.wait_ge(*bank_read(p))
            na_scores(0)
            for u in range(T * H):
                if u + 1 < T * H:
                    na_scores(u + 1)
                t, h = divmod(u, H)
                pe.wait_ge(s_ex, u + 1)
                transposes(("nap", t, h), [Pb[u % 2][:, b * P:(b + 1) * P] for b in range(2 if t in (0, T - 1) else 3)])
                if u > 0:
                    na_values(u - 1)
            na_values(T * H - 1)

            for t in range(T):
                pe.wait_ge(s_kn, t + 1)
                pe.wait_ge(s_qr, t + 1)
                for name, buf in (("k", k_sb), ("q", q_sb)):
                    for b in range(2):
                        transposes((name, t, b), [buf[:, t, 4 * b + j, :] for j in range(4)])

            def scores(u):
                t, h = divmod(u, H)
                pe.wait_ge(s_ex, T * H + u - 1)
                nc.tensor.matmul(SB[u % 2][:, :], qT[:, h, t * P:(t + 1) * P], kT[:, h, :],
                                 start=True, stop=True).then_inc(s_S, 1)

            def values(u):
                t, h = divmod(u, H)
                if h == 0:
                    pe.wait_ge(s_oe, T + t - 1)
                pe.wait_ge(s_PT[u % 2], (T * H + u) // 2 + 1)
                for k in range(T):
                    last = nc.tensor.matmul(OB[t % 2][:, h * DV:(h + 1) * DV], PT[u % 2][:, k, :],
                                            v_sb[:, k, h * DV:(h + 1) * DV], start=(k == 0), stop=(k == T - 1))
                last.then_inc(s_pv[u % 2], 1)

            def mix_side(t, h):
                if h == 3:
                    pe.wait_ge(s_on, t + 1)
                    transposes(("mix", t, 0), four(o_lat[t % 2], 0))
                    transposes(("mix", t, 1), four(o_na[:, t, :], 0))
                if h == 4:
                    for b in range(2):
                        p = turn["mix", t, b]
                        pe.wait_ge(*bank_read(p))
                    if t > 0:
                        pe.wait_ge(s_lgr, t)
                        pe.wait_ge(s_cnt, t)
                    for b in range(2):
                        for k in range(KD):
                            last = nc.tensor.matmul(YB[b][:, :], mixT[:, k, :], w_o[:, k, b * 512:(b + 1) * 512],
                                                    start=(k == 0), stop=(k == KD - 1))
                        last.then_inc(s_y, 1)
                if h == 7:
                    pe.wait_ge(s_h2s, t + 1)
                    for b in range(2):
                        transposes(("h2", t, b), four(h2s, b))

            def router(t):
                for b in range(2):
                    p = turn["h2", t, b]
                    pe.wait_ge(*bank_read(p))
                for k in range(KD):
                    last = nc.tensor.matmul(YB[0][:, 0:G + E], h2T[:, k, :], w_r_sb[:, k, :],
                                            start=(k == 0), stop=(k == KD - 1))
                last.then_inc(s_lg, 1)

            def ranks(t):
                pe.wait_ge(s_sel, t + 1)
                for i in range(t + 1):
                    last = nc.tensor.matmul(YB[1][:, 0:E], konst[:, K_ONE:K_ONE + P] if i < t else konst[:, K_TRI:K_TRI + P],
                                            sels[:, i, 0:E], start=(i == 0), stop=(i == t))
                last.then_inc(s_rank, 1)

            for t in range(T):
                for name in ("k", "q"):
                    for b in range(2):
                        p = turn[name, t, b]
                        pe.wait_ge(*bank_read(p))
            pe.wait_ge(s_wo, 16)
            pe.wait_ge(s_wr, 16)
            pe.wait_ge(s_k, 16)
            scores(0)
            for u in range(T * H):
                if u + 1 < T * H:
                    scores(u + 1)
                t, h = divmod(u, H)
                pe.wait_ge(s_ex, T * H + u + 1)
                transposes(("p", t, h), [Pb[u % 2][:, k * P:(k + 1) * P] for k in range(T)])
                if u > 0:
                    values(u - 1)
                if t > 0:
                    mix_side(t - 1, h)
                if t > 1 and h == 0:
                    router(t - 2)
                if t > 1 and h == 1:
                    ranks(t - 2)
            values(T * H - 1)
            router(T - 2)
            for h in range(H):
                mix_side(T - 1, h)
                if h == 3:
                    ranks(T - 2)
            router(T - 1)
            ranks(T - 1)
            pe.wait_ge(s_lgr, T)
            for t in range(T):
                last = nc.tensor.matmul(YB[0][:, 64:64 + E], konst[:, K_ONE:K_ONE + P], sels[:, t, 0:E],
                                        start=(t == 0), stop=(t == T - 1))
            last.then_inc(s_counted, 1)
            for p in (len(order) - 2, len(order) - 1):
                pe.wait_ge(*bank_read(p))

            def pass_pe(j):
                pe.wait_ge(s_hot, T * (j + 1))
                if j > 0:
                    pe.wait_ge(s_hid, E * j)
                for e in range(E):
                    for t in range(T):
                        last = nc.tensor.matmul(GU[1][:, 3 * e:3 * e + 3], hot[t][:, e, :], digits[:, 3 * t:3 * t + 3],
                                                start=(t == 0), stop=(t == T - 1))
                last.then_inc(s_ix, 1)

                def bank_free(n):
                    if not isinstance(n, int) or n >= 2:
                        pe.wait_ge(s_te, n - 1)

                def turn_rows(e, par, half):
                    g = E * j + e
                    pe.wait_ge(s_xg[par], 16 * (half + E // 2 * j + 1))
                    v = xg[par].rearrange("s (p k) -> s k p", k=KD)
                    for b in range(2):
                        bank_free(turn_x(g, b))
                        for i in range(4):
                            last = nc.tensor.transpose(x_bank(e, par, b)[:, i * P:(i + 1) * P], v[:, 4 * b + i, :], ident)
                        last.then_inc(s_tt, 1)

                def down(e, par, half):
                    g = E * j + e
                    pe.wait_ge(s_te, turn_h(g) + 1)
                    pe.wait_ge(s_wdn[par], 16 * (half + E // 2 * j + 1))
                    if not isinstance(g, int) or g >= 2:
                        pe.wait_ge(s_ya, g - 1)
                        pe.wait_ge(s_yv, g - 1)
                    for b in range(2):
                        for k in range(2):
                            last = nc.tensor.matmul(YR[par][b][:, :], hidT[par][:, k, :],
                                                    w_dn[par][:, k, b * 512:(b + 1) * 512],
                                                    start=(k == 0), stop=(k == 1))
                        last.then_inc(s_dn, 1)

                def step(e, par, half):
                    g = E * j + e
                    pe.wait_ge(s_te, turn_x(g, 1) + 1)
                    pe.wait_ge(s_wgu[par], 32 * (half + E // 2 * j + 1))
                    if not isinstance(g, int) or g >= 2:
                        pe.wait_ge(s_hid, g - 1)
                    for i in range(2):
                        for k in range(KD):
                            last = nc.tensor.matmul(GU[par][:, i * F:(i + 1) * F], xT[par][:, k, :], w_gu[par][:, i, k, :],
                                                    start=(k == 0), stop=(k == KD - 1))
                    last.then_inc(s_gu, 1)
                    if not final(e):
                        turn_rows(e + 1, 1 - par, half + par)
                    if not first(e):
                        down(e - 1, 1 - par, half - 1 + par)
                    pe.wait_ge(s_hid, g + 1)
                    bank_free(turn_h(g))
                    v = hid[par].rearrange("s (p k) -> s k p", k=2)
                    for i in range(2):
                        last = nc.tensor.transpose(TPB[par][:, i * P:(i + 1) * P], v[:, i, :], ident)
                    last.then_inc(s_tt, 1)

                turn_rows(0, 0, 0)
                experts(pe, step)
                down(E - 1, 1, E // 2 - 1)

            pe.wait_ge(s_digits, 1)
            def extra_pe(i):
                g, par = E + i, (E + i) % 2
                turns, turn_hid = extra_turns(g)
                pe.wait_ge(s_hot, T * (i + 2))
                pe.wait_ge(s_hid, g)
                for t in range(T):
                    last = nc.tensor.matmul(GU[1][:, 0:3], hot[t][:, 0, :], digits[:, 3 * t:3 * t + 3],
                                            start=(t == 0), stop=(t == T - 1))
                last.then_inc(s_ix, 1)
                pe.wait_ge(s_xg[par], 16 * (g // 2 + 1))
                v = xg[par].rearrange("s (p k) -> s k p", k=KD)
                for b, n in enumerate(turns):
                    pe.wait_ge(s_te, n - 1)
                    for k in range(4):
                        last = nc.tensor.transpose(TPB[n % 2][:, k * P:(k + 1) * P], v[:, 4 * b + k, :], ident)
                    last.then_inc(s_tt, 1)
                pe.wait_ge(s_te, turns[1] + 1)
                pe.wait_ge(s_wgu[par], 32 * (g // 2 + 1))
                for w in range(2):
                    for k in range(KD):
                        last = nc.tensor.matmul(GU[par][:, w * F:(w + 1) * F], xT[par][:, k, :], w_gu[par][:, w, k, :],
                                                start=(k == 0), stop=(k == KD - 1))
                last.then_inc(s_gu, 1)
                pe.wait_ge(s_hid, g + 1)
                v = hid[par].rearrange("s (p k) -> s k p", k=2)
                for k in range(2):
                    last = nc.tensor.transpose(TPB[turn_hid % 2][:, k * P:(k + 1) * P], v[:, k, :], ident)
                last.then_inc(s_tt, 1)
                pe.wait_ge(s_te, turn_hid + 1)
                pe.wait_ge(s_wdn[par], 16 * (g // 2 + 1))
                pe.wait_ge(s_ya, g)
                pe.wait_ge(s_yv, g)
                for b in range(2):
                    for k in range(2):
                        last = nc.tensor.matmul(YR[par][b][:, :], hidT[par][:, k, :],
                                                w_dn[par][:, k, b * 512:(b + 1) * 512],
                                                start=(k == 0), stop=(k == 1))
                    last.then_inc(s_dn, 1)

            passes(pe, pass_pe, extra_pe)


def kernel(**inputs):
    from concourse import bacc
    from concourse.bass_utils import run_bass_kernel_spmd

    a = {k: np.asarray(v) for k, v in inputs.items()}
    f32 = np.float32
    one = np.ones(P, f32)

    def by_feature(g):
        return g.reshape(-1, P).T

    def padded(*parts):
        return np.concatenate([*parts, one])[:P].reshape(P, 1)

    cols = np.concatenate([
        by_feature(a["g_mix_norm"][0]), by_feature(a["g_q_a"][0]), by_feature(a["g_kv_a"][0]),
        by_feature(a["g_mla_out"][0]), by_feature(a["g_na_out"][0]), by_feature(a["g_ffn_norm"][0]),
        padded(a["g_mla_q"][0][:NOPE]), padded(a["g_mla_k"][0][:NOPE]),
        padded(a["g_na_q"][0], a["g_na_q"][0]), padded(a["g_na_k"][0], a["g_na_k"][0]),
        a["g_ffn_norm"][0].reshape(P, KD)], axis=1)
    rows = np.concatenate([
        a["g_mla_q"][0][NOPE:], a["g_mla_k"][0][NOPE:],
        np.array([1 / Q_LORA, 1 / KV_LORA, 1 / ROPE, 1 / NOPE, 1 / ROPE, 1 / NOPE], f32),
        a["b_router_group"][0], a["b_router_expert"][0]]).reshape(1, NROW)

    def tiled(v):
        return np.ascontiguousarray(v.reshape(ROWS, T, TCOLS, -1).transpose(1, 2, 0, 3).reshape(T, P, -1))

    inv = ROPE_BASE ** (-np.arange(ROPE // 4, dtype=f32) / (ROPE // 4))
    tok = np.arange(SEQ)
    ang = np.stack([(tok // GRID_W)[:, None] * inv, (tok % GRID_W)[:, None] * inv], axis=1)
    cos = np.stack([np.cos(ang), np.cos(ang)], axis=2).reshape(SEQ, ROPE)
    sin = np.stack([-np.sin(ang), np.sin(ang)], axis=2).reshape(SEQ, ROPE)
    rope = np.stack([tiled(cos.astype(f32)), tiled(sin.astype(f32))]).transpose(0, 2, 1, 3)

    p = np.arange(P, dtype=f32)
    konst = np.concatenate([
        np.triu(np.ones((P, P), f32), 1), np.ones((P, P), f32), np.tile(p + 1, (P, 1)),
        np.tile(p[:E], (P, 1)),
        np.stack([np.stack([p, np.full(P, t, f32), one], axis=1) for t in range(T)], axis=1).reshape(P, 3 * T)], axis=1)

    arrays = {
        "x": tiled(a["x"][0]), "cols": cols, "rows": rows, "rope": rope, "ident": np.eye(P, dtype=f32),
        "rpb": np.pad(a["na_rpb"].reshape(-1), RPB_PAD)[::-1], "consts": konst, "w_in": a["w_in"][0], "w_qb": a["w_q_b"][0],
        "w_kvb": a["w_kv_b"][0], "w_out": a["w_out"][0],
        "w_r": np.concatenate([a["w_router_group"][0], a["w_router_expert"][0]], axis=1)
        .reshape(KD, P, G + E).transpose(1, 0, 2),
        "w_gate": a["w_gate"][0], "w_up": a["w_up"][0], "w_down": a["w_down"][0],
    }
    arrays = {"in_" + k: np.ascontiguousarray(v) for k, v in arrays.items()}
    nc = bacc.Bacc("TRN2", target_bir_lowering=False, num_devices=1)
    args = [nc.dram_tensor(k, v.shape, mybir.dt.float32, kind="ExternalInput").ap() for k, v in arrays.items()]
    out = nc.dram_tensor("out", (T, P, D_MODEL), mybir.dt.float32, kind="ExternalOutput").ap()
    build(nc, *args, out)
    r = run_bass_kernel_spmd(nc, [arrays], core_ids=[0])
    y = r.results[0]["out"]
    return y.reshape(T, TCOLS, ROWS, D_MODEL).transpose(2, 0, 1, 3).reshape(1, SEQ, D_MODEL)
```
